# Optimizing a Trainium2 kernel written in Bass

```python
import math
import jax, jax.numpy as jnp
from jax import lax
import numpy as np

D_MODEL = 1024
BATCH = 1
SEQ = 256
DEPTH = 2

N_A_LAYERS = DEPTH // 2
N_B_LAYERS = DEPTH - N_A_LAYERS
N_DENSE_FFN = (DEPTH + 1) // 2
N_MOE_FFN = DEPTH // 2

RET_HEADS = 4
RET_QK_DIM = D_MODEL // RET_HEADS
RET_V_DIM = 2 * D_MODEL // RET_HEADS
RET_CHUNK = 128

DIFF_HEADS = 8
DIFF_HEAD_DIM = D_MODEL // DIFF_HEADS // 2
DIFF_V_DIM = 2 * DIFF_HEAD_DIM
Q_BLOCK = 128

D_FF_DENSE = 2816
N_EXPERTS = 8
TOP_K = 2
D_FF_EXPERT = 3584

ROPE_THETA = 10000.0
NORM_EPS = 1e-6
SUBLN_EPS = 1e-5

kernel_name = "yoco_retention_diffattn_moe_trunk"

def rms_norm(x, g, eps=NORM_EPS):
    xf = x.astype(jnp.float32)
    y = (xf * lax.rsqrt(jnp.mean(xf * xf, axis=-1, keepdims=True) + eps)).astype(x.dtype)
    return y if g is None else y * g

def rope_tables(seq, dim, dtype):
    inv = 1.0 / (ROPE_THETA ** (jnp.arange(0, dim, 2, dtype=jnp.float32) / dim))
    ang = jnp.arange(seq, dtype=jnp.float32)[:, None] * inv[None, :]
    ang = jnp.concatenate([ang, ang], axis=-1)
    return jnp.cos(ang).astype(dtype), jnp.sin(ang).astype(dtype)

def apply_rope(x, cos, sin):
    x1, x2 = jnp.split(x, 2, axis=-1)
    return x * cos + jnp.concatenate([-x2, x1], axis=-1) * sin

def retention(h, w_in, w_out):
    B, S, D = h.shape
    H, dk, dv, C = RET_HEADS, RET_QK_DIM, RET_V_DIM, RET_CHUNK
    dt = h.dtype
    proj = h @ w_in
    q, k, v, g = jnp.split(proj, [D, 2 * D, 4 * D], axis=-1)
    q = q.reshape(B, S, H, dk).transpose(0, 2, 1, 3)
    k = k.reshape(B, S, H, dk).transpose(0, 2, 1, 3)
    v = v.reshape(B, S, H, dv).transpose(0, 2, 1, 3)
    cos, sin = rope_tables(S, dk, dt)
    q = apply_rope(q, cos, sin)
    k = apply_rope(k, cos, sin) * (dk ** -0.5)

    log_gamma = jnp.log1p(-jnp.exp2(-5.0 - jnp.arange(H, dtype=jnp.float32)))
    pos = jnp.arange(C, dtype=jnp.float32)
    rel = pos[:, None] - pos[None, :]
    intra_decay = jnp.where(rel >= 0, jnp.exp(log_gamma[:, None, None] * jnp.maximum(rel, 0.0)), 0.0).astype(dt)
    q_decay = jnp.exp(log_gamma[:, None] * (pos + 1.0)).astype(dt)
    k_decay = jnp.exp(log_gamma[:, None] * (C - 1.0 - pos)).astype(dt)
    chunk_decay = jnp.exp(log_gamma * C).astype(dt)

    N = S // C
    qc = q.reshape(B, H, N, C, dk)
    kc = k.reshape(B, H, N, C, dk)
    vc = v.reshape(B, H, N, C, dv)
    scores = jnp.einsum('bhncd,bhnkd->bhnck', qc, kc) * intra_decay[None, :, None]
    intra = jnp.einsum('bhnck,bhnke->bhnce', scores, vc)

    def step(state, xs):
        qi, ki, vi = xs
        inter_i = jnp.einsum('bhcd,bhde->bhce', qi, state) * q_decay[None, :, :, None]
        state = state * chunk_decay[None, :, None, None] + jnp.einsum(
            'bhcd,bhce->bhde', ki * k_decay[None, :, :, None], vi)
        return state, inter_i

    state0 = jnp.zeros((B, H, dk, dv), dt)
    _, inter = lax.scan(step, state0, (qc.transpose(2, 0, 1, 3, 4),
                                        kc.transpose(2, 0, 1, 3, 4),
                                        vc.transpose(2, 0, 1, 3, 4)))
    inter = inter.transpose(1, 2, 0, 3, 4)
    o = (intra + inter).reshape(B, H, S, dv).transpose(0, 2, 1, 3)
    o = rms_norm(o, None).reshape(B, S, H * dv)
    return (jax.nn.silu(g) * o) @ w_out

def shared_kv(x, kv_norm_g, w_kv):
    B, S, _ = x.shape
    H, d = DIFF_HEADS, DIFF_HEAD_DIM
    kv = rms_norm(x, kv_norm_g) @ w_kv
    k, v = jnp.split(kv, [H * 2 * d], axis=-1)
    k = k.reshape(B, S, H, 2, d).transpose(0, 2, 3, 1, 4)
    cos, sin = rope_tables(S, d, x.dtype)
    k = apply_rope(k, cos, sin)
    v = v.reshape(B, S, H, DIFF_V_DIM).transpose(0, 2, 1, 3)
    return k, v

def diff_attention(h, k, v, w_q, lam_q1, lam_k1, lam_q2, lam_k2, subln_g, w_o, lambda_init):
    B, S, _ = h.shape
    H, d, C = DIFF_HEADS, DIFF_HEAD_DIM, Q_BLOCK
    q = (h @ w_q).reshape(B, S, H, 2, d).transpose(0, 2, 3, 1, 4)
    cos, sin = rope_tables(S, d, h.dtype)
    q = apply_rope(q, cos, sin) * (d ** -0.5)
    lam = (jnp.exp(jnp.sum(lam_q1.astype(jnp.float32) * lam_k1.astype(jnp.float32)))
           - jnp.exp(jnp.sum(lam_q2.astype(jnp.float32) * lam_k2.astype(jnp.float32)))
           + lambda_init)
    nq = S // C
    qb = q.reshape(B, H, 2, nq, C, d).transpose(3, 0, 1, 2, 4, 5)
    key_pos = jnp.arange(S)
    neg = jnp.finfo(jnp.float32).min

    def block(args):
        qi, bi = args
        logits = jnp.einsum('bhpcd,bhpsd->bhpcs', qi, k).astype(jnp.float32)
        qpos = bi * C + jnp.arange(C)
        mask = key_pos[None, :] <= qpos[:, None]
        a = jax.nn.softmax(jnp.where(mask, logits, neg), axis=-1)
        attn = a[:, :, 0] - lam * a[:, :, 1]
        return jnp.einsum('bhcs,bhse->bhce', attn.astype(v.dtype), v)

    out = lax.map(block, (qb, jnp.arange(nq)))
    out = out.transpose(1, 0, 3, 2, 4).reshape(B, S, H, DIFF_V_DIM)
    out = rms_norm(out, subln_g, SUBLN_EPS) * (1.0 - lambda_init)
    return out.reshape(B, S, H * DIFF_V_DIM) @ w_o

def swiglu(h, w_gate, w_up, w_down):
    return (jax.nn.silu(h @ w_gate) * (h @ w_up)) @ w_down

def moe_swiglu(h, w_router, w_gate, w_up, w_down):
    B, S, D = h.shape
    t = h.reshape(B * S, D)
    logits = (t @ w_router).astype(jnp.float32)
    top_vals, top_idx = lax.top_k(logits, TOP_K)
    top_w = jax.nn.softmax(top_vals, axis=-1)
    gates = jnp.sum(jax.nn.one_hot(top_idx, N_EXPERTS, dtype=jnp.float32) * top_w[..., None], axis=1)
    gates = gates.astype(t.dtype)
    out = jnp.zeros_like(t)
    for e in range(N_EXPERTS):
        out = out + swiglu(t, w_gate[e], w_up[e], w_down[e]) * gates[:, e:e + 1]
    return out.reshape(B, S, D)

def setup_inputs(seed: int = 0) -> dict:
    key = jax.random.key(seed)
    ks = jax.random.split(key, 24)
    D, f32 = D_MODEL, jnp.float32

    def nrm(k, shape, fan_in, scale=1.0):
        return jax.random.normal(k, shape, f32) * (scale * fan_in ** -0.5)

    out_scale = (2.0 * DEPTH) ** -0.5
    return {
        "x": jax.random.normal(ks[0], (BATCH, SEQ, D), f32),
        "attn_norm_g": 1.0 + 0.02 * jax.random.normal(ks[1], (DEPTH, D), f32),
        "ffn_norm_g": 1.0 + 0.02 * jax.random.normal(ks[2], (DEPTH, D), f32),
        "ret_w_in": nrm(ks[3], (N_A_LAYERS, D, 6 * D), D),
        "ret_w_out": nrm(ks[4], (N_A_LAYERS, 2 * D, D), 2 * D, out_scale),
        "kv_norm_g": 1.0 + 0.02 * jax.random.normal(ks[5], (D,), f32),
        "w_kv": nrm(ks[6], (D, DIFF_HEADS * 2 * DIFF_HEAD_DIM + DIFF_HEADS * DIFF_V_DIM), D),
        "diff_w_q": nrm(ks[7], (N_B_LAYERS, D, DIFF_HEADS * 2 * DIFF_HEAD_DIM), D),
        "diff_lam_q1": 0.1 * jax.random.normal(ks[8], (N_B_LAYERS, DIFF_HEAD_DIM), f32),
        "diff_lam_k1": 0.1 * jax.random.normal(ks[9], (N_B_LAYERS, DIFF_HEAD_DIM), f32),
        "diff_lam_q2": 0.1 * jax.random.normal(ks[10], (N_B_LAYERS, DIFF_HEAD_DIM), f32),
        "diff_lam_k2": 0.1 * jax.random.normal(ks[11], (N_B_LAYERS, DIFF_HEAD_DIM), f32),
        "diff_subln_g": 1.0 + 0.02 * jax.random.normal(ks[12], (N_B_LAYERS, DIFF_V_DIM), f32),
        "diff_w_o": nrm(ks[13], (N_B_LAYERS, DIFF_HEADS * DIFF_V_DIM, D), DIFF_HEADS * DIFF_V_DIM, out_scale),
        "ffn_w_gate": nrm(ks[14], (N_DENSE_FFN, D, D_FF_DENSE), D),
        "ffn_w_up": nrm(ks[15], (N_DENSE_FFN, D, D_FF_DENSE), D),
        "ffn_w_down": nrm(ks[16], (N_DENSE_FFN, D_FF_DENSE, D), D_FF_DENSE, out_scale),
        "moe_w_router": nrm(ks[17], (N_MOE_FFN, D, N_EXPERTS), D),
        "moe_w_gate": nrm(ks[18], (N_MOE_FFN, N_EXPERTS, D, D_FF_EXPERT), D),
        "moe_w_up": nrm(ks[19], (N_MOE_FFN, N_EXPERTS, D, D_FF_EXPERT), D),
        "moe_w_down": nrm(ks[20], (N_MOE_FFN, N_EXPERTS, D_FF_EXPERT, D), D_FF_EXPERT, out_scale),
        "final_norm_g": 1.0 + 0.02 * jax.random.normal(ks[21], (D,), f32),
    }

def reference(x, attn_norm_g, ffn_norm_g, ret_w_in, ret_w_out, kv_norm_g, w_kv,
              diff_w_q, diff_lam_q1, diff_lam_k1, diff_lam_q2, diff_lam_k2, diff_subln_g, diff_w_o,
              ffn_w_gate, ffn_w_up, ffn_w_down,
              moe_w_router, moe_w_gate, moe_w_up, moe_w_down, final_norm_g):
    k_sh = None
    v_sh = None
    for i in range(DEPTH):
        h = rms_norm(x, attn_norm_g[i])
        if i < N_A_LAYERS:
            x = x + retention(h, ret_w_in[i], ret_w_out[i])
        else:
            j = i - N_A_LAYERS
            lambda_init = 0.8 - 0.6 * math.exp(-0.3 * i)
            x = x + diff_attention(h, k_sh, v_sh, diff_w_q[j], diff_lam_q1[j], diff_lam_k1[j],
                                   diff_lam_q2[j], diff_lam_k2[j], diff_subln_g[j], diff_w_o[j],
                                   lambda_init)
        h = rms_norm(x, ffn_norm_g[i])
        if i % 2 == 0:
            x = x + swiglu(h, ffn_w_gate[i // 2], ffn_w_up[i // 2], ffn_w_down[i // 2])
        else:
            x = x + moe_swiglu(h, moe_w_router[i // 2], moe_w_gate[i // 2],
                               moe_w_up[i // 2], moe_w_down[i // 2])
        if i == N_A_LAYERS - 1:
            k_sh, v_sh = shared_kv(x, kv_norm_g, w_kv)
    return rms_norm(x, final_norm_g)


_drawn_inputs = setup_inputs


def setup_inputs(seed=0):
    import zlib

    import numpy as np

    out = dict(_drawn_inputs(seed))
    spreads = {}
    factors = {'kv_norm_g': 4.198,
     'diff_lam_k1': 8.0,
     'diff_lam_q2': 8.0,
     'diff_subln_g': 5.987,
     'final_norm_g': 2.753}
    for name, (base, spread) in spreads.items():
        noise = np.random.default_rng([zlib.crc32(name.encode()), seed]).standard_normal(out[name].shape)
        drawn = base * np.exp(spread * noise) if base else spread * noise
        out[name] = __import__('jax').numpy.asarray(drawn.astype(out[name].dtype))
    for name, factor in factors.items():
        out[name] = (out[name] * factor).astype(out[name].dtype)
    return out
```

```python
import math
from contextlib import ExitStack

import numpy as np
import concourse.bass as bass
from concourse import mybir

F32, F32R, I32, U32 = mybir.dt.float32, mybir.dt.float32r, mybir.dt.int32, mybir.dt.uint32
ALU = mybir.AluOpType
ACT = mybir.ActivationFunctionType
AX_X = mybir.AxisListType.X

P = 128
D = 1024
SEQ = 256
TILES = SEQ // P
KC = D // P
RET_H, RET_DK, RET_DV = 4, 256, 512
DIFF_H, DIFF_D, DIFF_V = 8, 64, 128
F_DENSE, F_EXPERT, N_EXPERTS = 2816, 3584, 8
NORM_EPS, SUBLN_EPS = 1e-6, 1e-5
LAMBDA_INIT = 0.8 - 0.6 * math.exp(-0.3)
ROPE_THETA = 10000.0
BLK = 512
UNIT = 2048
RAW_SLOTS = 6
SPLIT_SLOTS = 3
AHEAD = SPLIT_SLOTS - 1
NEG = -3.4028234663852886e38

G0, G1, U0, U1, C0, C1, T0, T1 = range(8)

CONST_PARTS = [("ident", P), ("before", P), ("ones", P), ("iota", P), ("causal", P),
               ("ret_cos", 2 * P), ("ret_sin", 2 * P), ("diff_cos", 2 * 32), ("diff_sin", 2 * 32),
               ("decay", RET_H * 3 * P), ("minus_half", 16)]
CONST_AT, _at = {}, 0
for _name, _width in CONST_PARTS:
    CONST_AT[_name] = (_at, _width)
    _at += _width
CONST_WIDTH = _at


def constant_table():
    f = np.float32
    tab = np.zeros((P, CONST_WIDTH), f)

    def put(name, a):
        at, width = CONST_AT[name]
        tab[:, at:at + width] = np.asarray(a, f).reshape(P, width)

    p = np.arange(P)
    put("ident", np.eye(P))
    put("before", p[:, None] < p[None, :])
    put("ones", np.ones((P, P)))
    put("iota", np.broadcast_to(p, (P, P)))
    put("causal", np.where(p[None, :] <= p[:, None], 0.0, NEG))
    put("minus_half", np.full((P, 16), -0.5))
    for name, dim in (("ret", RET_DK), ("diff", DIFF_D)):
        inv = f(1.0) / (f(ROPE_THETA) ** (np.arange(0, dim, 2, dtype=f) / f(dim)))
        ang = np.arange(SEQ, dtype=f)[:, None] * inv[None, :]
        for fn, kind in ((np.cos, "cos"), (np.sin, "sin")):
            put(f"{name}_{kind}", fn(ang).astype(f).reshape(TILES, P, dim // 2).transpose(1, 0, 2))
    lg = np.log1p(-np.exp2(-5.0 - np.arange(RET_H)))
    rel = np.arange(SEQ)[None, :] - p[:, None]
    m = np.where(rel >= 0, np.exp(lg[:, None, None] * np.maximum(rel, 0)), 0.0) * RET_DK ** -0.5
    put("decay", np.concatenate([m, m[:, :, :P]], axis=2).transpose(1, 0, 2))
    return tab


def ffn_blocks():
    return [(c, min(BLK, F_DENSE - c)) for c in range(0, F_DENSE, BLK)]


RET_ORDER = [(kind, n) for pair in range(RET_H // 2)
             for kind, n in (("q", pair), ("k", pair), ("g", 2 * pair), ("g", 2 * pair + 1),
                             ("v", 2 * pair), ("v", 2 * pair + 1))]
RET_COL = {"q": 0, "k": D, "v": 2 * D, "g": 4 * D}
KVQ_ORDER = [("k", 0), ("k", 1), ("q", 0), ("q", 1), ("v", 0), ("v", 1)]
STEPS = F_EXPERT // BLK
ITEM_UNITS = STEPS * 6
PAIRS = DIFF_H // 2


class Order:

    def __init__(self):
        self.n, self.done, self.unit_done = 0, {}, []
        self.bank, self.free, self.last = {}, {}, [None] * 8

    def open(self, key, bank, read, known_free=False):
        self.bank[key], self.free[key] = bank, None if known_free else self.last[bank]
        self.last[bank] = read

    def group(self, key):
        self.n += 1
        self.done[key] = self.n

    def unit(self, *keys):
        self.n += 1
        self.unit_done.append(self.n)
        for key in keys:
            self.done[key] = self.n


def work_order():
    o = Order()

    def both(key, bank, sem, base):
        for t in range(TILES):
            o.open((*key, t), bank + t, (sem, base + t + 1))

    def turn(key, sem, base):
        both(key, T0, sem, base)
        for t in range(TILES):
            o.group((*key, t))

    def norm_turn(n):
        for g in range(4):
            o.open(("norm_turn", n, g), T0 + g % 2, ("norm_lo", 4 * n + g + 1))
            o.group(("norm_turn", n, g))

    def units(key, n):
        for u in range(n):
            if u == n - 1:
                o.group((*key, 0))
                o.unit((*key, 1))
            else:
                o.unit()

    def pv(h):
        both(("ret_pv", h), C0, "ret_y", 2 * h)
        for t in range(TILES):
            o.group(("ret_pv", h, t))

    norm_turn(0)
    seen = {"q": 0, "k": 0}
    for j, (kind, n) in enumerate(RET_ORDER):
        pair, stage = divmod(j, 6)
        if kind in "qk":
            both(("ret", j), (G0, U0)[j % 2], "rope_read", 2 * (2 * pair + stage))
        else:
            both(("ret", j), (G0, U0)[j % 2], "ret_gate" if kind == "g" else "ret_v", 2 * n)
        units(("ret", j), 2)
        if stage == 0 and pair:
            pv(1)
        if stage in (1, 2):
            turn(("ret_turn", stage - 1, pair), "ret_turned", 2 * (2 * pair + stage - 1))
            if pair:
                turn(("y_turn", stage - 1), "y_lo", 2 * (stage - 1))
        if stage == 3:
            for h in (2 * pair, 2 * pair + 1):
                o.open(("ret_score", h), T0 + h % 2, ("ret_p", h + 1))
                o.group(("ret_score", h))
        if stage == 5:
            pv(2 * pair)
    for h in range(RET_H):
        if h == 0:
            for c in range(2):
                both(("ret_out", c), (G0, U0)[c], "x_sum", 2 * c)
        o.unit()
        if h < RET_H - 1:
            o.unit()
        else:
            o.group(("ret_out", 0, 0)); o.group(("ret_out", 0, 1)); o.group(("ret_out", 1, 0))
            o.unit(("ret_out", 1, 1))
        if h == 0:
            pv(3)
            turn(("y_turn", 2), "y_lo", 4)
        if h == 1:
            turn(("y_turn", 3), "y_lo", 6)
    norm_turn(1)
    blocks = ffn_blocks()
    for s in range(len(blocks) + 1):
        now = s < len(blocks)
        n = blocks[s][1] * KC // UNIT if now else 0
        if now:
            both(("gate", s), G0, "ffn_sil", 2 * s)
            for u in range(n - 1):
                o.unit()
        if s:
            turn(("hid_turn", s - 1), "hid_lo", 2 * (s - 1))
        if now:
            o.group(("gate", s, 0))
            o.unit(("gate", s, 1))
        for c in range(2):
            if s:
                both(("down", s - 1, c), C0, "x_sum", 4 + 4 * (s - 1) + 2 * c)
                units(("down", s - 1, c), 1)
            if now and c == 0:
                both(("up", s), U0, "ffn_hid", 2 * s)
                units(("up", s), n)
    norm_turn(2)

    def logits(hp):
        for a in range(2):
            o.open(("logits", hp, 1, a), C0 + a, ("exp_done", 8 * hp + 2 * a + 2))
            o.group(("logits", hp, 1, a))
        o.open(("logits", hp, 0), T1, ("exp_done", 8 * hp + 8))
        o.group(("logits", hp, 0))

    for j, (kind, n) in enumerate(KVQ_ORDER):
        both(("kvq", j), (G0, U0)[j % 2], *(("kv_v", 2 * n) if kind == "v" else ("kvq_read", 2 * j)))
        units(("kvq", j), 2)
        if j == 0:
            norm_turn(3)
        if 1 <= j <= 4:
            for t in range(TILES):
                o.open(("kvq_turn", j - 1, t), T0 + t,
                       ("kvq_turned", 2 * (j - 1) + t + 1 if j < 3 else 4 * (j - 2) + 2 * t + 2))
            for t in range(TILES):
                o.group(("kvq_turn", j - 1, t))
        if j == 4:
            logits(0)
    for hp in range(PAIRS):
        if hp + 1 < PAIRS:
            logits(hp + 1)
        for t in (1, 0):
            o.open(("attn_turn", hp, t), T0, ("attn_turned", 2 * hp + 2 - t))
            o.group(("attn_turn", hp, t))
            if hp % 2 == 0:
                o.open(("attn_out", hp // 2, t), (G0, U0)[t] + hp // 2, ("attn_o", hp // 2 * 2 + t + 1))
            if hp % 2:
                o.group(("attn_out", hp // 2, t))
    for half in range(2):
        turn(("o_turn", half), "o_lo", 2 * half)
    for c, bank in enumerate((C0, G0)):
        both(("wo", c), bank, "x_sum", 28 + 2 * c)
        units(("wo", c), 2)
    for g in range(4):
        o.open(("norm_turn", 4, g), T0 + g % 2, ("router_x", g + 1))
        o.group(("norm_turn", 4, g))
    o.open(("router",), T0, ("router_read", 1))
    o.group(("router",))
    o.open(("places",), T1, ("places_read", 1))
    o.group(("places",))

    def gather(key, base):
        for g, bank in enumerate((G1, U1)):
            o.open((*key, g), bank, ("xe_lo", base + g + 1))
            o.group((*key, g))

    def hidden(key, bank, read):
        o.open(key, bank, read)
        o.unit()
        o.unit(key)

    def combine(key, base, known_free):
        for q in range(4):
            o.open((*key, q), (G1, U1)[q % 2], ("comb", base + q + 1), known_free=known_free and q < 2)
            o.group((*key, q))

    gather(("gather",), 0)
    hidden(("e_gate", 0), G0, ("e_sil", 1))
    hidden(("e_up", 0), U0, ("e_hid", 1))
    start = (o.n, len(o.unit_done))

    def item(at, last):
        for s in range(1, STEPS + 1):
            if not (last and s == STEPS):
                hidden((at, "e_gate", s), G0, ("e_sil", s + 1))
            o.open((at, "e_turn", s - 1), T0, ("e_turn_lo", s), known_free=True)
            o.group((at, "e_turn", s - 1))
            if s == 1:
                combine((at, "combine"), 0, True)
            if not (last and s == STEPS):
                hidden((at, "e_up", s), U0, ("e_hid", s + 1))
            if s == 1:
                o.open((at, "slots"), T1, ("slots_read", 2), known_free=True)
                o.group((at, "slots"))
                for c in range(2):
                    o.open((at, "e_down", c), C0 + c, ("os_lo", 2 + c + 1), known_free=True)
            if s == STEPS - 1 and not last:
                gather((at, "gather_next"), 2)
            if s < STEPS:
                o.unit()
                o.unit()
            else:
                o.unit()
                o.group((at, "e_down", 0))
                o.unit((at, "e_down", 1))
        if last:
            combine((at, "combine_last"), 4, False)

    banks = list(o.last)
    item("item", False)
    per_item = o.n - start[0]
    assert len(o.unit_done) - start[1] == ITEM_UNITS
    o.n, o.last = start[0], banks
    o.item_units = o.unit_done[start[1]:]
    del o.unit_done[start[1]:]
    item("last", True)
    o.last_units = o.unit_done[start[1]:]
    return o, per_item


def stream(nc, ins, out, table):
    order, pe_per_item = work_order()
    T = {}
    dense_sources = []

    def units_of(w, col, n, kc0=0, kcs=KC):
        v = w.rearrange("(c p) n -> p c n", p=P)
        kk = min(UNIT // n, kcs)
        return [(v[:, k:k + kk, col:col + n], kk, n) for k in range(kc0, kc0 + kcs, kk)]

    w_in, w_out = ins["ret_w_in"][0], ins["ret_w_out"][0]
    w_gate, w_up, w_down = ins["ffn_w_gate"][0], ins["ffn_w_up"][0], ins["ffn_w_down"][0]
    w_kv, w_q, w_o = ins["w_kv"], ins["diff_w_q"][0], ins["diff_w_o"][0]
    for kind, n in RET_ORDER:
        dense_sources += units_of(w_in, RET_COL[kind] + n * BLK, BLK)
    dense_sources += units_of(w_out, 0, D, 0, 2 * KC)
    blocks = ffn_blocks()
    for s in range(len(blocks) + 1):
        if s < len(blocks):
            dense_sources += units_of(w_gate, *blocks[s])
        for c in range(2):
            if s:
                col, n = blocks[s - 1]
                dense_sources += units_of(w_down, c * BLK, BLK, col // P, n // P)
            if s < len(blocks) and c == 0:
                dense_sources += units_of(w_up, *blocks[s])
    for kind, n in KVQ_ORDER:
        w, col = {"k": (w_kv, 0), "v": (w_kv, D), "q": (w_q, 0)}[kind]
        dense_sources += units_of(w, col + n * BLK, BLK)
    for c in range(2):
        dense_sources += units_of(w_o, c * BLK, BLK)
    n_dense = len(dense_sources)
    first_loop_unit = n_dense + 4
    assert len(order.unit_done) == first_loop_unit + ITEM_UNITS - 4
    assert ITEM_UNITS % RAW_SLOTS == 0 and ITEM_UNITS % SPLIT_SLOTS == 0

    PER_ITEM = {"pe_done": pe_per_item, "hi_ready": ITEM_UNITS, "lo_ready": ITEM_UNITS,
                "e_sil": STEPS, "e_hid": STEPS, "e_turn_hi": STEPS, "e_turn_lo": STEPS,
                "xe_hi": 2, "xe_lo": 2, "os_hi": 2, "os_lo": 2, "slots_read": 2, "comb": 4,
                "cur": 1, "choose": 2}
    PER_ITEM["raw_in"] = 16 * (ITEM_UNITS // RAW_SLOTS)

    with ExitStack() as ctx:
        def sb(name, shape, dt=F32):
            return ctx.enter_context(nc.sbuf_tensor(name, shape, dt))

        raw = sb("raw", [P, RAW_SLOTS, UNIT])
        w_hi = sb("w_hi", [P, SPLIT_SLOTS, UNIT], F32R)
        w_lo = sb("w_lo", [P, SPLIT_SLOTS, UNIT], F32R)
        actA_hi, actA_lo = sb("actA_hi", [P, UNIT], F32R), sb("actA_lo", [P, UNIT], F32R)
        actB_hi, actB_lo = sb("actB_hi", [P, UNIT], F32R), sb("actB_lo", [P, UNIT], F32R)
        x = sb("x_sb", [P, TILES, D])
        gains = sb("gains", [P, 2, D])
        const = sb("const", [P, CONST_WIDTH])
        work = sb("work", [P, 12544])
        stat = sb("stat", [P, 3, 9 * TILES + 2 * DIFF_H])
        soft = sb("soft", [P, 2 * PAIRS, 5, 4])
        lam_in = sb("lam_in", [P, 4, DIFF_D])
        lam = sb("lam", [P, 8])
        sub_gain = sb("sub_gain", [P, 2])
        w_router = sb("w_router", [P, KC, N_EXPERTS])
        top = sb("top", [P, 160])
        top_at = sb("top_at", [P, TILES, 8], U32)
        trips = sb("trips", [P, 1], I32)
        psum = ctx.enter_context(nc.psum_tensor("psum", [P, 8, BLK], F32))

        sem = {}
        for name in (["pe_done", "hi_ready", "lo_ready", "x_in", "const_in", "small_in", "out_done", "down_asked"]
                     + [f"raw_in{r}" for r in range(RAW_SLOTS)] + [f"gain_in{n}" for n in range(6)]
                     + ["sum_sq", "var", "rstd", "hn", "norm_hi", "norm_lo", "x_sum", "dve_step",
                        "rope_read_1", "rope_read", "roped", "ret_turned", "ret_p", "ret_gate", "ret_v", "ret_y",
                        "y_hi", "y_lo", "ffn_sil", "ffn_hid", "hid_hi", "hid_lo",
                        "q_zeroed", "kvq_read_1", "kvq_read", "kvq_roped", "kvq_turned", "kv_v", "lam_dot", "lam_exp",
                        "max_ready", "exp_done", "attn", "attn_turned", "o_sq", "attn_o", "o_hi", "o_lo",
                        "router_x", "router_read", "gap", "gap_exp", "chosen", "places_read", "routed",
                        "cur", "choose", "xe_hi", "xe_lo", "e_sil", "e_hid", "e_turn_hi", "e_turn_lo",
                        "slots_read", "os_hi", "os_lo", "comb"]):
            sem[name] = ctx.enter_context(nc.semaphore(name))
        sem["raw_in"] = [sem[f"raw_in{r}"] for r in range(RAW_SLOTS)]
        sem["gain_in"] = [sem[f"gain_in{n}"] for n in range(6)]

        class Count:

            def __init__(self):
                self.item = None

            def at(self, name, n):
                per = PER_ITEM.get(name)
                return n if self.item is None or per is None else self.item * per + n

            def pe(self, *key):
                return self.at("pe_done", order.done[key])

        def c_(name, lo=0, n=None):
            at, width = CONST_AT[name]
            return const[:, at + lo:at + (width if n is None else lo + n)]

        def bank(key):
            return psum[:, order.bank[key], :]

        def area(at, *shape):
            size = int(np.prod(shape))
            v = work[:, at:at + size]
            if len(shape) == 2:
                v = v.rearrange("p (a b) -> p a b", a=shape[0])
            if len(shape) == 3:
                v = v.rearrange("p (a b c) -> p a b c", a=shape[0], b=shape[1])
            return v

        def chunks(t, n=SEQ):
            return t[:, :].rearrange("p (c n) -> p c n", n=n)

        def wide(ap, n):
            p_, b_ = ap.shape
            return ap.rearrange("p (o b) -> p o b", o=1).to_broadcast([p_, n, b_])

        r_rope = [area(0, TILES, BLK), area(1024, TILES, BLK)]
        r_ropeA, r_ropeB = area(2048, BLK), area(2560, BLK)
        r_T = [area(3072, 4, SEQ), area(4096, 4, SEQ)]
        r_p = area(5120, 2, 3 * P)
        r_v = area(5888, 2, TILES, BLK)
        r_y = area(7936, TILES, RET_H * RET_DV)
        r_junk = area(12032, BLK)
        norm_junk = area(11264, D)
        f_sil, f_hid = area(0, TILES, BLK), area(1024, TILES, BLK)
        a_kT = area(0, DIFF_H, SEQ)
        a_qT = area(2048, 2, DIFF_H, SEQ)
        a_v = area(6144, TILES, D)
        a_ropeA, a_ropeB = area(8192, BLK), area(8704, BLK)
        a_rope = area(9216, 2, TILES, BLK)
        a_e = [area(9216, 4, P), area(8192, 4, SEQ)]
        a_a = [area(10240, 2, P), area(9728, 2, SEQ)]
        a_aT = [area(11008, 2, P), area(10496, 4, P)]
        a_o, a_junk = area(0, TILES, D), area(2048, BLK)
        e_xT = area(2048, KC, SEQ)
        e_choose, e_sil, e_hid = area(4096, TILES, P), area(4352, BLK), area(4864, BLK)
        e_route, e_cur, e_weight = area(5376, 4, 2 * N_EXPERTS), area(5440, 4), area(5444, 1)
        hn_at = [5888, 5888, 0, 6144, 0, 6144]
        hn = [area(at, TILES, D) for at in hn_at]
        xe_hi, xe_lo = actA_hi[:, 0:D], actA_lo[:, 0:D]
        eT_hi, eT_lo = actB_hi[:, 0:BLK], actB_lo[:, 0:BLK]
        os_hi, os_lo = actB_hi[:, BLK:BLK + D], actB_lo[:, BLK:BLK + D]
        slots = actB_hi[:, BLK + D:BLK + D + SEQ]

        RSTD = ["attn", "y0", "y1", "y2", "y3", "ffn0", "kvq", "sub", "ffn1", "final"]
        SUM_SQ = {"attn": 2, "y0": 4, "y1": 6, "y2": 8, "y3": 10, "ffn0": 12, "kvq": 14, "ffn1": 16, "final": 18}
        WIDTH = {"sub": 2 * DIFF_H}

        def stats(row, name, col=0, n=1):
            at = sum(WIDTH.get(before, TILES) for before in RSTD[:RSTD.index(name)]) + col
            return stat[:, row, at:at + n]

        def sums(name, col=0, n=1):
            return stats(0, name, col, n)

        def rstd(name, col=0, n=1):
            return stats(2, name, col, n)

        x_dram = ins["x"].rearrange("b (t p) d -> p (b t) d", p=P)
        out_dram = out.rearrange("b (t p) d -> p (b t) d", p=P)
        e_w = {"gate": ins["moe_w_gate"].rearrange("l e (c p) n -> (l e) p c n", p=P),
               "up": ins["moe_w_up"].rearrange("l e (c p) n -> (l e) p c n", p=P),
               "down": ins["moe_w_down"].rearrange("l e (c p) n -> (l e) p c n", p=P)}
        block = ctx.enter_context(nc.Block())

        @block.sync
        def _(sp):
            w = Count()
            for t in range(TILES):
                sp.dma_start(x[:, t, :], x_dram[:, t, :]).then_inc(sem["x_in"], 16)
            sp.dma_start(const[:, :], table).then_inc(sem["const_in"], 16)

            def load(u, src, kk, n, waited=False):
                if u >= RAW_SLOTS and not waited:
                    sp.wait_ge(sem["lo_ready"], w.at("lo_ready", u - RAW_SLOTS + 1))
                dst = raw[:, u % RAW_SLOTS, 0:kk * n].rearrange("p (k n) -> p k n", k=kk)
                sp.dma_start(dst, src).then_inc(sem["raw_in"][u % RAW_SLOTS], 16)

            def load_block(u, kind, expert, s):
                v = e_w[kind][expert]
                for half in range(2):
                    if kind == "down":
                        if s == half == 0:
                            sp.wait_ge(sem["lo_ready"], w.at("lo_ready", u - RAW_SLOTS + 1))
                            sp.sem_inc(sem["down_asked"], 1)
                        load(u + half, v[:, 4 * s + 2 * half:4 * s + 2 * half + 2, :], 2, D, s == half == 0)
                    else:
                        load(u + half, v[:, 4 * half:4 * half + 4, s * BLK:(s + 1) * BLK], 4, BLK)

            for u, (src, kk, n) in enumerate(dense_sources):
                load(u, src, kk, n)
            load_block(n_dense, "gate", 0, 0)
            load_block(n_dense + 2, "up", 0, 0)
            sp.wait_ge(sem["routed"], 1)
            trip = sp.value_load(trips[0:1, 0:1], min_val=N_EXPERTS - 1, max_val=2 * N_EXPERTS - 1)

            def item(i, last):
                u = first_loop_unit
                for s in range(1, STEPS + 1):
                    if s < STEPS:
                        load_block(u, "gate", i % N_EXPERTS, s)
                        load_block(u + 2, "up", i % N_EXPERTS, s)
                        u += 4
                    elif not last:
                        load_block(u, "gate", (i + 1) % N_EXPERTS, 0)
                        load_block(u + 2, "up", (i + 1) % N_EXPERTS, 0)
                        u += 4
                    load_block(u, "down", i % N_EXPERTS, s - 1)
                    u += 2

            with sp.Fori(0, trip) as i:
                w.item = i
                item(i, False)
            w.item = trip
            item(trip, True)
            for t in range(TILES):
                sp.wait_ge(sem["hn"], 2 * 5 + t + 1)
                sp.dma_start(out_dram[:, t, :], hn[5][:, t, :]).then_inc(sem["out_done"], 16)
            sp.wait_ge(sem["out_done"], 16 * TILES)

        @block.gpsimd
        def _(pool):
            w = Count()
            gain_rows = [ins["attn_norm_g"][0:1, :], ins["ffn_norm_g"][0:1, :],
                         ins["kv_norm_g"].rearrange("(o d) -> o d", o=1), ins["attn_norm_g"][1:2, :],
                         ins["ffn_norm_g"][1:2, :], ins["final_norm_g"].rearrange("(o d) -> o d", o=1)]

            def load_gain(n):
                if n >= 2:
                    pool.wait_ge(sem["hn"], 2 * (n - 2) + 2)
                pool.dma_start(gains[:, n % 2, :], gain_rows[n].to_broadcast([P, D])).then_inc(sem["gain_in"][n], 16)

            def root(name):
                r, n = RSTD.index(name), WIDTH.get(name, TILES)
                pool.wait_ge(sem["var"], r + 1)
                nc.gpsimd.tensor_tensor(stats(2, name, 0, n), stats(1, name, 0, n), c_("minus_half", 0, n),
                                        ALU.pow).then_inc(sem["rstd"], 1)

            load_gain(0)
            load_gain(1)
            for n, name in enumerate(("diff_lam_q1", "diff_lam_k1", "diff_lam_q2", "diff_lam_k2")):
                pool.dma_start(lam_in[:, n, :], ins[name].to_broadcast([P, DIFF_D])).then_inc(sem["small_in"], 16)
            pool.dma_start(sub_gain[:, 0:1], ins["diff_subln_g"].rearrange("o d -> d o")).then_inc(sem["small_in"], 16)
            pool.dma_start(w_router[:, :, :], ins["moe_w_router"][0].rearrange("(c p) e -> p c e", p=P)
                           ).then_inc(sem["small_in"], 16)
            pool.wait_ge(sem["const_in"], 16)
            root("attn")
            load_gain(2)
            for h in range(RET_H):
                root(f"y{h}")
            root("ffn0")
            load_gain(3)
            pool.wait_ge(sem["ffn_hid"], 1)
            nc.gpsimd.memset(a_qT[64:128, 0, :, :], 0.0).then_inc(sem["q_zeroed"], 1)
            nc.gpsimd.memset(a_qT[0:64, 1, :, :], 0.0).then_inc(sem["q_zeroed"], 1)
            pool.wait_ge(sem["q_zeroed"], 2)
            root("kvq")
            load_gain(4)
            load_gain(5)
            root("sub")
            root("ffn1")
            root("final")

        @block.scalar
        def _(act):
            w = Count()
            split = [0]

            def hi_through(limit):
                for u in range(split[0], limit):
                    size = dense_sources[u][1] * dense_sources[u][2] if u < n_dense else UNIT
                    act.wait_ge(sem["raw_in"][u % RAW_SLOTS], w.at("raw_in", 16 * (u // RAW_SLOTS + 1)))
                    if u >= SPLIT_SLOTS:
                        act.wait_ge(sem["pe_done"], w.at("pe_done", unit_done(u - SPLIT_SLOTS)))
                    nc.scalar.copy(w_hi[:, u % SPLIT_SLOTS, 0:size], raw[:, u % RAW_SLOTS, 0:size]
                                   ).then_inc(sem["hi_ready"], 1)
                split[0] = max(split[0], limit)

            unit_list = order.unit_done[:first_loop_unit] + order.item_units

            def unit_done(u):
                return unit_list[u]

            def square_sums(name):
                for t in range(TILES):
                    if name == "attn":
                        act.wait_ge(sem["x_in"], 16 * TILES)
                    elif name == "final":
                        act.wait_ge(sem["comb"], w.at("comb", 4 + 2 * t + 2))
                    else:
                        act.wait_ge(sem["x_sum"], {"ffn0": 4, "kvq": 28, "ffn1": 32}[name] - 1 + t)
                    if t:
                        act.wait_ge(sem["sum_sq"], SUM_SQ[name] - 1)
                    nc.scalar.activation(norm_junk, x[:, t, :], ACT.Square, accum_out=sums(name, t)
                                         ).then_inc(sem["sum_sq"], 1)

            def norm_hi(n, dst):
                v = chunks(dst)
                for g in range(4):
                    t, half = divmod(g, 2)
                    act.wait_ge(sem["pe_done"], w.pe("norm_turn", n, g))
                    nc.scalar.copy(v[:, 4 * half:4 * half + 4, t * P:(t + 1) * P],
                                   bank(("norm_turn", n, g)).rearrange("p (c n) -> p c n", c=4)
                                   ).then_inc(sem["norm_hi"], 1)

            square_sums("attn")
            hi_through(AHEAD)
            norm_hi(0, actA_hi)
            used = 0

            def y_sums(h):
                for t in range(TILES):
                    act.wait_ge(sem["pe_done"], w.pe("ret_pv", h, t))
                    if 2 * h + t:
                        act.wait_ge(sem["sum_sq"], SUM_SQ["attn"] + 2 * h + t)
                    nc.scalar.activation(r_junk, bank(("ret_pv", h, t)), ACT.Square, accum_out=sums(f"y{h}", t)
                                         ).then_inc(sem["sum_sq"], 1)

            def y_hi(h):
                v = chunks(actB_hi)
                for t in range(TILES):
                    act.wait_ge(sem["pe_done"], w.pe("y_turn", h, t))
                    nc.scalar.copy(v[:, 4 * (h % 2):4 * (h % 2) + 4, t * P:(t + 1) * P],
                                   bank(("y_turn", h, t)).rearrange("p (c n) -> p c n", c=4)
                                   ).then_inc(sem["y_hi"], 1)

            for j, (kind, n) in enumerate(RET_ORDER):
                pair, stage = divmod(j, 6)
                used += 2
                hi_through(used + AHEAD)
                for t in range(TILES):
                    if kind == "g":
                        act.wait_ge(sem["pe_done"], w.pe("ret", j, t))
                        nc.scalar.activation(r_y[:, t, n * RET_DV:(n + 1) * RET_DV], bank(("ret", j, t)), ACT.Silu
                                             ).then_inc(sem["ret_gate"], 1)
                    if kind == "v":
                        act.wait_ge(sem["pe_done"], w.pe("ret", j, t))
                        nc.scalar.copy(r_v[:, n % 2, t, :], bank(("ret", j, t))).then_inc(sem["ret_v"], 1)
                if stage == 0 and pair:
                    y_sums(1)
                if stage in (1, 2):
                    for t in range(TILES):
                        act.wait_ge(sem["pe_done"], w.pe("ret_turn", stage - 1, pair, t))
                        nc.scalar.copy(r_T[stage - 1][:, :, t * P:(t + 1) * P],
                                       bank(("ret_turn", stage - 1, pair, t)).rearrange("p (c n) -> p c n", c=4)
                                       ).then_inc(sem["ret_turned"], 1)
                    if pair:
                        y_hi(stage - 1)
                if stage == 5:
                    y_sums(2 * pair)
            for h in range(RET_H):
                used += 1
                hi_through(used + AHEAD)
                used += 1
                hi_through(used + AHEAD)
                if h == 0:
                    y_sums(3)
                    y_hi(2)
                if h == 1:
                    y_hi(3)
            square_sums("ffn0")
            norm_hi(1, actA_hi)
            for s in range(len(blocks) + 1):
                now = s < len(blocks)
                n = blocks[s][1] * KC // UNIT if now else 0
                if s:
                    width = blocks[s - 1][1]
                    used += max(n - 1, 0)
                    hi_through(used + AHEAD)
                    for t in range(TILES):
                        act.wait_ge(sem["pe_done"], w.pe("hid_turn", s - 1, t))
                        nc.scalar.copy(chunks(actB_hi)[:, 0:width // P, t * P:(t + 1) * P],
                                       bank(("hid_turn", s - 1, t))[:, 0:width].rearrange("p (c n) -> p c n", n=P)
                                       ).then_inc(sem["hid_hi"], 1)
                    used += min(n, 1)
                else:
                    used += n
                hi_through(used + AHEAD)
                if now:
                    for t in range(TILES):
                        act.wait_ge(sem["pe_done"], w.pe("gate", s, t))
                        if s:
                            act.wait_ge(sem["ffn_hid"], 2 * (s - 1) + t + 1)
                        width = blocks[s][1]
                        nc.scalar.activation(f_sil[:, t, 0:width], bank(("gate", s, t))[:, 0:width], ACT.Silu
                                             ).then_inc(sem["ffn_sil"], 1)
                if s:
                    used += 2
                used += n
                hi_through(used + AHEAD)
            square_sums("kvq")
            act.wait_ge(sem["lam_dot"], 2)
            nc.scalar.activation(lam[:, 2:4], lam[:, 0:2], ACT.Exp).then_inc(sem["lam_exp"], 1)
            norm_hi(2, actA_hi)

            def exps(hp, t):
                st = soft[:, 2 * hp + t, :, :]
                act.wait_ge(sem["max_ready"], 2 * hp + 2 - t)
                if hp:
                    act.wait_ge(sem["attn"], 4 * (hp - 1) + (2 if t else 4))
                for m in range(4):
                    key = ("logits", hp, 1, m // 2) if t else ("logits", hp, 0)
                    src = bank(key)[:, m % 2 * SEQ:(m % 2 + 1) * SEQ] if t else bank(key)[:, m * P:(m + 1) * P]
                    nc.scalar.activation(a_e[t][:, m, :], src, ACT.Exp, bias=st[:, 1, m:m + 1],
                                         scale=DIFF_D ** -0.5, accum_out=st[:, 2, m:m + 1]
                                         ).then_inc(sem["exp_done"], 1)

            for j, (kind, n) in enumerate(KVQ_ORDER):
                used += 2
                hi_through(used + AHEAD)
                if kind == "v":
                    for t in range(TILES):
                        act.wait_ge(sem["pe_done"], w.pe("kvq", j, t))
                        nc.scalar.copy(a_v[:, t, n * BLK:(n + 1) * BLK], bank(("kvq", j, t))).then_inc(sem["kv_v"], 1)
                if j == 0:
                    norm_hi(3, actB_hi)
                if 1 <= j <= 4:
                    m = j - 1
                    for t in range(TILES):
                        act.wait_ge(sem["pe_done"], w.pe("kvq_turn", m, t))
                        src = bank(("kvq_turn", m, t)).rearrange("p (c n) -> p c n", c=4)
                        heads, cols = slice(4 * (m % 2), 4 * (m % 2) + 4), slice(t * P, (t + 1) * P)
                        if m < 2:
                            nc.scalar.copy(a_kT[:, heads, cols], src).then_inc(sem["kvq_turned"], 1)
                        else:
                            act.wait_ge(sem["q_zeroed"], 2)
                            nc.scalar.copy(a_qT[0:64, 0, heads, cols], src[0:64]).then_inc(sem["kvq_turned"], 1)
                            nc.scalar.copy(a_qT[64:128, 1, heads, cols], src[64:128]).then_inc(sem["kvq_turned"], 1)
                if j == 4:
                    exps(0, 1)
                    exps(0, 0)
            for hp in range(PAIRS):
                if hp + 1 < PAIRS:
                    exps(hp + 1, 1)
                    exps(hp + 1, 0)
                for t in (1, 0):
                    n = 4 if t else 2
                    act.wait_ge(sem["pe_done"], w.pe("attn_turn", hp, t))
                    nc.scalar.copy(a_aT[t], bank(("attn_turn", hp, t))[:, 0:n * P].rearrange("p (c n) -> p c n", c=n)
                                   ).then_inc(sem["attn_turned"], 1)
            for half in range(2):
                for t in range(TILES):
                    act.wait_ge(sem["pe_done"], w.pe("attn_out", half, t))
                    if 2 * half + t:
                        act.wait_ge(sem["o_sq"], 2 * (2 * half + t))
                    nc.scalar.activation(a_junk, bank(("attn_out", half, t)), ACT.Square).then_inc(sem["o_sq"], 1)
            for half in range(2):
                for t in range(TILES):
                    act.wait_ge(sem["pe_done"], w.pe("o_turn", half, t))
                    nc.scalar.activation(chunks(actA_hi)[:, 4 * half:4 * half + 4, t * P:(t + 1) * P],
                                         bank(("o_turn", half, t)).rearrange("p (c n) -> p c n", c=4),
                                         ACT.Copy, scale=sub_gain[:, 1:2]).then_inc(sem["o_hi"], 1)
            used += 4
            hi_through(used + AHEAD)
            square_sums("ffn1")
            for g in range(4):
                t, half = divmod(g, 2)
                act.wait_ge(sem["pe_done"], w.pe("norm_turn", 4, g))
                nc.scalar.copy(e_xT[:, 4 * half:4 * half + 4, t * P:(t + 1) * P],
                               bank(("norm_turn", 4, g)).rearrange("p (c n) -> p c n", c=4)
                               ).then_inc(sem["router_x"], 1)
            act.wait_ge(sem["gap"], 1)
            nc.scalar.activation(top[:, 34:36], top[:, 32:34], ACT.Exp).then_inc(sem["gap_exp"], 1)

            def gathered(key, count):
                for g in range(2):
                    act.wait_ge(sem["pe_done"], w.pe(*key, g))
                    nc.scalar.copy(xe_hi[:, g * BLK:(g + 1) * BLK], bank((*key, g))).then_inc(sem["xe_hi"], 1)

            def silu(key, s):
                act.wait_ge(sem["pe_done"], w.pe(*key))
                if s:
                    act.wait_ge(sem["e_hid"], w.at("e_hid", s))
                nc.scalar.activation(e_sil, bank(key), ACT.Silu).then_inc(sem["e_sil"], 1)

            gathered(("gather",), 0)
            used += 2
            hi_through(used + AHEAD)
            silu(("e_gate", 0), 0)
            used += 2
            hi_through(used + AHEAD)
            act.wait_ge(sem["routed"], 1)
            trip = act.value_load(trips[0:1, 0:1], min_val=N_EXPERTS - 1, max_val=2 * N_EXPERTS - 1)

            def item(at, last):
                used, end = first_loop_unit, first_loop_unit + ITEM_UNITS - (4 if last else 0)
                limit = end if last else end + AHEAD
                for s in range(1, STEPS + 1):
                    if not (last and s == STEPS):
                        used += 2
                        hi_through(min(used + AHEAD, limit))
                        silu((at, "e_gate", s), s)
                    act.wait_ge(sem["pe_done"], w.pe(at, "e_turn", s - 1))
                    nc.scalar.copy(eT_hi, bank((at, "e_turn", s - 1))).then_inc(sem["e_turn_hi"], 1)
                    if not (last and s == STEPS):
                        used += 2
                    hi_through(min(used + AHEAD, limit))
                    if s == 1:
                        act.wait_ge(sem["pe_done"], w.pe(at, "slots"))
                        nc.scalar.copy(slots, bank((at, "slots"))[:, 0:SEQ]).then_inc(sem["slots_read"], 1)
                        nc.scalar.copy(e_weight, bank((at, "slots"))[:, SEQ:SEQ + 1]).then_inc(sem["slots_read"], 1)
                    if s == STEPS - 1 and not last:
                        gathered((at, "gather_next"), 2)
                    used += 2
                    hi_through(min(used + AHEAD, limit))
                for c in range(2):
                    act.wait_ge(sem["pe_done"], w.pe(at, "e_down", c))
                    act.wait_ge(sem["slots_read"], w.at("slots_read", 2))
                    nc.scalar.activation(os_hi[:, c * BLK:(c + 1) * BLK], bank((at, "e_down", c)), ACT.Copy,
                                         scale=e_weight).then_inc(sem["os_hi"], 1)

            with act.Fori(0, trip) as i:
                w.item = i
                item("item", False)
            w.item = trip
            split[0] = first_loop_unit + AHEAD
            unit_list[first_loop_unit:] = order.last_units
            item("last", True)
            square_sums("final")

        @block.vector
        def _(dve):
            w = Count()
            split, steps = [0], [0]
            as_f32 = lambda v: v.bitcast(F32)

            def lo_through(limit):
                for u in range(split[0], limit):
                    size = dense_sources[u][1] * dense_sources[u][2] if u < n_dense else UNIT
                    dve.wait_ge(sem["hi_ready"], w.at("hi_ready", u + 1))
                    slot = u % SPLIT_SLOTS
                    nc.vector.tensor_tensor(w_lo[:, slot, 0:size], raw[:, u % RAW_SLOTS, 0:size],
                                            as_f32(w_hi[:, slot, 0:size]), ALU.subtract).then_inc(sem["lo_ready"], 1)
                split[0] = max(split[0], limit)

            def step(ins):
                steps[0] += 1
                ins.then_inc(sem["dve_step"], 1)
                dve.wait_ge(sem["dve_step"], steps[0])

            def mean_square(name, size, eps):
                r, n = RSTD.index(name), WIDTH.get(name, TILES)
                if name in SUM_SQ:
                    dve.wait_ge(sem["sum_sq"], SUM_SQ[name])
                nc.vector.tensor_scalar(stats(1, name, 0, n), stats(0, name, 0, n), 1.0 / size, eps,
                                        ALU.mult, ALU.add).then_inc(sem["var"], 1)

            def norm(n, name):
                dve.wait_ge(sem["gain_in"][n], 16)
                dve.wait_ge(sem["rstd"], RSTD.index(name) + 1)
                for t in range(TILES):
                    nc.vector.scalar_tensor_tensor(hn[n][:, t, :], x[:, t, :], rstd(name, t), gains[:, n % 2, :],
                                                   ALU.mult, ALU.mult).then_inc(sem["hn"], 1)

            def norm_lo(n, hi, lo):
                for g in range(4):
                    t, half = divmod(g, 2)
                    dve.wait_ge(sem["norm_hi"], 4 * n + g + 1)
                    part = (slice(None), slice(4 * half, 4 * half + 4), slice(t * P, (t + 1) * P))
                    nc.vector.tensor_tensor(chunks(lo)[part], bank(("norm_turn", n, g)).rearrange("p (c n) -> p c n", c=4),
                                            as_f32(chunks(hi)[part]), ALU.subtract).then_inc(sem["norm_lo"], 1)

            def add_to_x(key, t, c, count):
                dve.wait_ge(sem["pe_done"], w.pe(*key))
                if count > 4:
                    dve.wait_ge(sem["x_sum"], count - 4)
                v = x[:, t, c * BLK:(c + 1) * BLK]
                nc.vector.tensor_tensor(v, v, bank(key), ALU.add).then_inc(sem["x_sum"], 1)

            mean_square("attn", D, NORM_EPS)
            norm(0, "attn")
            lo_through(AHEAD)
            norm_lo(0, actA_hi, actA_lo)
            used = 0

            def rope(key, m, t, half, cos, sin, A, B, dst, read_once, read, done):
                dve.wait_ge(sem["pe_done"], w.pe(*key))
                if m:
                    dve.wait_ge(done, m)
                n = BLK // (2 * half)
                src = bank(key)
                s4 = src.rearrange("p (h two d) -> p h two d", two=2, d=half)
                b4 = B.rearrange("p (h two d) -> p h two d", two=2, d=half)
                nc.vector.tensor_tensor(A.rearrange("p (h d) -> p h d", d=half),
                                        src.rearrange("p (h d) -> p h d", d=half),
                                        wide(cos, 2 * n), ALU.mult).then_inc(read_once, 1)
                nc.vector.scalar_tensor_tensor(b4[:, :, 0, :], s4[:, :, 1, :], -1.0, wide(sin, n),
                                               ALU.mult, ALU.mult).then_inc(read_once, 1)
                nc.vector.tensor_tensor(b4[:, :, 1, :], s4[:, :, 0, :], wide(sin, n), ALU.mult).then_inc(read, 1)
                dve.wait_ge(read_once, 2 * m + 2)
                dve.wait_ge(read, m + 1)
                nc.vector.tensor_tensor(dst, A, B, ALU.add).then_inc(done, 1)

            def make_y(h):
                mean_square(f"y{h}", RET_DV, NORM_EPS)
                dve.wait_ge(sem["rstd"], RSTD.index(f"y{h}") + 1)
                dve.wait_ge(sem["ret_gate"], 2 * h + 2)
                for t in range(TILES):
                    v = r_y[:, t, h * RET_DV:(h + 1) * RET_DV]
                    nc.vector.scalar_tensor_tensor(v, bank(("ret_pv", h, t)), rstd(f"y{h}", t), v,
                                                   ALU.mult, ALU.mult).then_inc(sem["ret_y"], 1)

            def y_lo(h):
                for t in range(TILES):
                    dve.wait_ge(sem["y_hi"], 2 * h + t + 1)
                    part = (slice(None), slice(4 * (h % 2), 4 * (h % 2) + 4), slice(t * P, (t + 1) * P))
                    nc.vector.tensor_tensor(chunks(actB_lo)[part], bank(("y_turn", h, t)).rearrange("p (c n) -> p c n", c=4),
                                            as_f32(chunks(actB_hi)[part]), ALU.subtract).then_inc(sem["y_lo"], 1)

            dve.wait_ge(sem["const_in"], 16)
            for j, (kind, n) in enumerate(RET_ORDER):
                pair, stage = divmod(j, 6)
                used += 2
                lo_through(used + AHEAD)
                if kind in "qk":
                    m = 2 * pair + stage
                    if pair:
                        dve.wait_ge(sem["pe_done"], w.pe("ret_turn", stage, 0, 1))
                    for t in range(TILES):
                        rope(("ret", j, t), 2 * m + t, t, RET_DK // 2, c_("ret_cos", t * P, P), c_("ret_sin", t * P, P),
                             r_ropeA, r_ropeB, r_rope[stage][:, t, :], sem["rope_read_1"], sem["rope_read"], sem["roped"])
                if stage == 0 and pair:
                    make_y(1)
                if stage in (1, 2) and pair:
                    y_lo(stage - 1)
                if stage == 3:
                    for h in (2 * pair, 2 * pair + 1):
                        dve.wait_ge(sem["pe_done"], w.pe("ret_score", h))
                        at, _ = CONST_AT["decay"]
                        nc.vector.tensor_tensor(r_p[:, h % 2, :], bank(("ret_score", h))[:, 0:3 * P],
                                                c_("decay", h * 3 * P, 3 * P), ALU.mult).then_inc(sem["ret_p"], 1)
                if stage == 5:
                    make_y(2 * pair)
            for h in range(RET_H):
                used += 2
                lo_through(used + AHEAD)
                if h == 0:
                    make_y(3)
                    y_lo(2)
                if h == 1:
                    y_lo(3)
            for c in range(2):
                for t in range(TILES):
                    add_to_x(("ret_out", c, t), t, c, 2 * c + t + 1)
            mean_square("ffn0", D, NORM_EPS)
            norm(1, "ffn0")
            norm_lo(1, actA_hi, actA_lo)
            for s in range(len(blocks) + 1):
                now = s < len(blocks)
                n = blocks[s][1] * KC // UNIT if now else 0
                if s:
                    width = blocks[s - 1][1]
                    used += max(n - 1, 0)
                    lo_through(used + AHEAD)
                    for t in range(TILES):
                        dve.wait_ge(sem["hid_hi"], 2 * (s - 1) + t + 1)
                        part = (slice(None), slice(0, width // P), slice(t * P, (t + 1) * P))
                        nc.vector.tensor_tensor(chunks(actB_lo)[part],
                                                bank(("hid_turn", s - 1, t))[:, 0:width].rearrange("p (c n) -> p c n", n=P),
                                                as_f32(chunks(actB_hi)[part]), ALU.subtract).then_inc(sem["hid_lo"], 1)
                    used += min(n, 1) + 1
                    lo_through(used + AHEAD)
                    for t in range(TILES):
                        add_to_x(("down", s - 1, 0, t), t, 0, 4 * s + t + 1)
                else:
                    used += n
                used += n
                lo_through(used + AHEAD)
                if now:
                    width = blocks[s][1]
                    for t in range(TILES):
                        dve.wait_ge(sem["pe_done"], w.pe("up", s, t))
                        dve.wait_ge(sem["ffn_sil"], 2 * s + t + 1)
                        nc.vector.tensor_tensor(f_hid[:, t, 0:width], f_sil[:, t, 0:width], bank(("up", s, t))[:, 0:width],
                                                ALU.mult).then_inc(sem["ffn_hid"], 1)
                if s:
                    used += 1
                    lo_through(used + AHEAD)
                    for t in range(TILES):
                        add_to_x(("down", s - 1, 1, t), t, 1, 4 * s + 2 + t + 1)
            mean_square("kvq", D, NORM_EPS)
            dve.wait_ge(sem["small_in"], 16 * 6)
            for m in range(2):
                step(nc.vector.tensor_tensor(lam_in[:, 2 * m, :], lam_in[:, 2 * m, :], lam_in[:, 2 * m + 1, :], ALU.mult))
                nc.vector.reduce_sum(lam[:, m:m + 1], lam_in[:, 2 * m, :], axis=AX_X).then_inc(sem["lam_dot"], 1)
            step(nc.vector.tensor_scalar(sub_gain[:, 1:2], sub_gain[:, 0:1], 1.0 - LAMBDA_INIT, None, ALU.mult))
            norm(2, "kvq")
            norm_lo(2, actA_hi, actA_lo)
            norm(3, "kvq")
            dve.wait_ge(sem["lam_exp"], 1)
            step(nc.vector.tensor_tensor(lam[:, 4:5], lam[:, 3:4], lam[:, 2:3], ALU.subtract))
            step(nc.vector.tensor_scalar(lam[:, 5:6], lam[:, 4:5], -LAMBDA_INIT, None, ALU.add))

            def largest(hp, t):
                st = soft[:, 2 * hp + t, :, :]
                if t:
                    dve.wait_ge(sem["pe_done"], w.pe("logits", hp, 1, 1))
                    v = psum[:, C0:C1 + 1, :].rearrange("p b (m n) -> p (b m) n", n=SEQ)
                else:
                    dve.wait_ge(sem["pe_done"], w.pe("logits", hp, 0))
                    v = bank(("logits", hp, 0)).rearrange("p (m n) -> p m n", n=P)
                own = v[:, :, t * P:(t + 1) * P]
                step(nc.vector.tensor_tensor(own, own, wide(c_("causal"), 4), ALU.add))
                step(nc.vector.tensor_reduce(st[:, 0, :], v, AX_X, ALU.max))
                nc.vector.tensor_scalar(st[:, 1, :], st[:, 0, :], -DIFF_D ** -0.5, None, ALU.mult
                                        ).then_inc(sem["max_ready"], 1)

            def differences(hp, t):
                st = soft[:, 2 * hp + t, :, :]
                dve.wait_ge(sem["exp_done"], 8 * hp + (4 if t else 8))
                step(nc.vector.reciprocal(st[:, 3, :], st[:, 2, :]))
                step(nc.vector.tensor_scalar(st[:, 4, :], st[:, 3, :], lam[:, 5:6], None, ALU.mult))
                if hp:
                    dve.wait_ge(sem["pe_done"], w.pe("attn_turn", hp - 1, t))
                for a in range(2):
                    e0, e1 = a_e[t][:, 2 * a, :], a_e[t][:, 2 * a + 1, :]
                    step(nc.vector.tensor_scalar(e1, e1, st[:, 4, 2 * a + 1:2 * a + 2], None, ALU.mult))
                    nc.vector.scalar_tensor_tensor(a_a[t][:, a, :], e0, st[:, 3, 2 * a:2 * a + 1], e1,
                                                   ALU.mult, ALU.add).then_inc(sem["attn"], 1)

            for j, (kind, n) in enumerate(KVQ_ORDER):
                used += 2
                lo_through(used + AHEAD)
                if j < 4:
                    if j >= 2:
                        dve.wait_ge(sem["pe_done"], w.pe("kvq_turn", j - 2, 1))
                    for t in range(TILES):
                        rope(("kvq", j, t), 2 * j + t, t, DIFF_D // 2, c_("diff_cos", t * 32, 32), c_("diff_sin", t * 32, 32),
                             a_ropeA, a_ropeB, a_rope[:, j % 2, t, :], sem["kvq_read_1"], sem["kvq_read"], sem["kvq_roped"])
                if j == 0:
                    norm_lo(3, actB_hi, actB_lo)
                if j == 4:
                    largest(0, 1)
                    largest(0, 0)
            for hp in range(PAIRS):
                if hp + 1 < PAIRS:
                    largest(hp + 1, 1)
                    largest(hp + 1, 0)
                differences(hp, 1)
                differences(hp, 0)
            for half in range(2):
                for t in range(TILES):
                    e = 2 * half + t
                    dve.wait_ge(sem["o_sq"], 2 * e + 1)
                    nc.vector.tensor_reduce(sums("sub", DIFF_H * t + 4 * half, 4), a_junk.rearrange("p (h n) -> p h n", h=4),
                                            AX_X, ALU.add).then_inc(sem["o_sq"], 1)
            dve.wait_ge(sem["o_sq"], 8)
            mean_square("sub", DIFF_V, SUBLN_EPS)
            dve.wait_ge(sem["rstd"], RSTD.index("sub") + 1)
            for half in range(2):
                for t in range(TILES):
                    dst = a_o[:, t, half * BLK:(half + 1) * BLK].rearrange("p (h n) -> p h n", h=4)
                    scale = rstd("sub", DIFF_H * t + 4 * half, 4).rearrange("p (h o) -> p h o", o=1).to_broadcast([P, 4, P])
                    nc.vector.tensor_tensor(dst, bank(("attn_out", half, t)).rearrange("p (h n) -> p h n", h=4), scale,
                                            ALU.mult).then_inc(sem["attn_o"], 1)
            for half in range(2):
                for t in range(TILES):
                    dve.wait_ge(sem["o_hi"], 2 * half + t + 1)
                    part = (slice(None), slice(4 * half, 4 * half + 4), slice(t * P, (t + 1) * P))
                    nc.vector.scalar_tensor_tensor(chunks(actA_lo)[part], bank(("o_turn", half, t)).rearrange("p (c n) -> p c n", c=4),
                                                   sub_gain[:, 1:2], as_f32(chunks(actA_hi)[part]),
                                                   ALU.mult, ALU.subtract).then_inc(sem["o_lo"], 1)
            for c in range(2):
                used += 2
                lo_through(used + AHEAD)
                for t in range(TILES):
                    add_to_x(("wo", c, t), t, c, 28 + 2 * c + t + 1)
            mean_square("ffn1", D, NORM_EPS)
            norm(4, "ffn1")
            dve.wait_ge(sem["pe_done"], w.pe("wo", 1, 1))
            nc.vector.memset(as_f32(slots), 0.0).then_inc(sem["dve_step"], 1)
            nc.vector.memset(as_f32(os_hi), 0.0).then_inc(sem["os_lo"], 1)
            nc.vector.memset(as_f32(os_lo), 0.0).then_inc(sem["os_lo"], 1)
            steps[0] += 1
            dve.wait_ge(sem["dve_step"], steps[0])

            lg = top[:, 0:16].rearrange("p (t e) -> p t e", t=TILES)
            mv = top[:, 16:32].rearrange("p (t e) -> p t e", t=TILES)
            gap, gap_e, w1, w2, at_f = top[:, 32:34], top[:, 34:36], top[:, 36:38], top[:, 38:40], top[:, 40:44]
            first, second, chosen, gate = (top[:, a:a + 16].rearrange("p (t e) -> p t e", t=TILES) for a in (44, 60, 76, 92))
            place = top[:, 108:124].rearrange("p (t e) -> p t e", t=TILES)
            busiest = top[:, 124:125]
            dve.wait_ge(sem["pe_done"], w.pe("router"))
            nc.vector.tensor_copy(top[:, 0:16], bank(("router",))[:, 0:16]).then_inc(sem["router_read"], 1)
            dve.wait_ge(sem["router_read"], 1)
            for t in range(TILES):
                step(nc.vector.max(mv[:, t, :], lg[:, t, :]))
                step(nc.vector.max_index(top_at[:, t, :], mv[:, t, :], lg[:, t, :]))
            nc.vector.tensor_tensor(gap, mv[:, :, 1], mv[:, :, 0], ALU.subtract).then_inc(sem["gap"], 1)
            step(nc.vector.tensor_copy(at_f.rearrange("p (t e) -> p t e", t=TILES), top_at[:, :, 0:2]))
            for t in range(TILES):
                step(nc.vector.tensor_scalar(first[:, t, :], c_("iota", 0, N_EXPERTS), at_f[:, 2 * t:2 * t + 1], None, ALU.is_equal))
                step(nc.vector.tensor_scalar(second[:, t, :], c_("iota", 0, N_EXPERTS), at_f[:, 2 * t + 1:2 * t + 2], None, ALU.is_equal))
            nc.vector.tensor_tensor(chosen, first, second, ALU.add).then_inc(sem["chosen"], 1)
            dve.wait_ge(sem["gap_exp"], 1)
            step(nc.vector.tensor_scalar(w2, gap_e, 1.0, None, ALU.add))
            step(nc.vector.reciprocal(w1, w2))
            step(nc.vector.tensor_tensor(w2, w1, gap_e, ALU.mult))
            for t in range(TILES):
                step(nc.vector.tensor_scalar(second[:, t, :], second[:, t, :], w2[:, t:t + 1], None, ALU.mult))
                step(nc.vector.scalar_tensor_tensor(gate[:, t, :], first[:, t, :], w1[:, t:t + 1], second[:, t, :],
                                                    ALU.mult, ALU.add))
            dve.wait_ge(sem["pe_done"], w.pe("places"))
            step(nc.vector.scalar_tensor_tensor(place, bank(("places",))[:, 0:16].rearrange("p (t e) -> p t e", t=TILES), 1.0,
                                                chosen, ALU.add, ALU.mult))
            step(nc.vector.tensor_reduce(busiest, bank(("places",))[:, 16:24], AX_X, ALU.max))
            step(nc.vector.tensor_scalar(top[:, 125:126], busiest, float(P), float(N_EXPERTS), ALU.is_gt, ALU.mult))
            step(nc.vector.tensor_scalar(e_route[:, 0:2, 0:N_EXPERTS], place, -1.0, None, ALU.add))
            step(nc.vector.tensor_scalar(e_route[:, 0:2, N_EXPERTS:], place, -1.0 - P, None, ALU.add))
            step(nc.vector.tensor_copy(e_route[:, 2:4, 0:N_EXPERTS], gate))
            step(nc.vector.tensor_copy(e_route[:, 2:4, N_EXPERTS:], gate))
            nc.vector.tensor_scalar(trips[:, :], top[:, 125:126], float(N_EXPERTS - 1), None, ALU.add
                                    ).then_inc(sem["routed"], 1)

            def choose(item, n):
                nc.vector.tensor_copy(e_cur, e_route[:, :, bass.ds(item, 1)].rearrange("p a b -> p (a b)")
                                      ).then_inc(sem["cur"], 1)
                dve.wait_ge(sem["cur"], w.at("cur", n + 1))
                for t in range(TILES):
                    nc.vector.tensor_scalar(e_choose[:, t, :], c_("iota"), e_cur[:, t:t + 1], None, ALU.is_equal
                                            ).then_inc(sem["choose"], 1)

            def gathered(key, count):
                for g in range(2):
                    dve.wait_ge(sem["xe_hi"], w.at("xe_hi", count + g + 1))
                    part = (slice(None), slice(g * BLK, (g + 1) * BLK))
                    nc.vector.tensor_tensor(xe_lo[part], bank((*key, g)), as_f32(xe_hi[part]), ALU.subtract
                                            ).then_inc(sem["xe_lo"], 1)

            def hidden(key, s):
                dve.wait_ge(sem["pe_done"], w.pe(*key))
                dve.wait_ge(sem["e_sil"], w.at("e_sil", s + 1))
                nc.vector.tensor_tensor(e_hid, e_sil, bank(key), ALU.mult).then_inc(sem["e_hid"], 1)

            def combined(key, count):
                for q in range(4):
                    t, c = divmod(q, 2)
                    dve.wait_ge(sem["pe_done"], w.pe(*key, q))
                    v = x[:, t, c * BLK:(c + 1) * BLK]
                    nc.vector.tensor_tensor(v, v, bank((*key, q)), ALU.add).then_inc(sem["comb"], 1)

            choose(0, 0)
            gathered(("gather",), 0)
            used += 2
            lo_through(used + AHEAD)
            used += 2
            lo_through(used + AHEAD)
            hidden(("e_up", 0), 0)
            dve.wait_ge(sem["routed"], 1)
            trip = dve.value_load(trips[0:1, 0:1], min_val=N_EXPERTS - 1, max_val=2 * N_EXPERTS - 1)

            def item(at, i, last):
                used, end = first_loop_unit, first_loop_unit + ITEM_UNITS - (4 if last else 0)
                limit = end if last else end + AHEAD
                for s in range(1, STEPS + 1):
                    if not (last and s == STEPS):
                        used += 2
                        lo_through(min(used + AHEAD, limit))
                    dve.wait_ge(sem["e_turn_hi"], w.at("e_turn_hi", s))
                    nc.vector.tensor_tensor(eT_lo, bank((at, "e_turn", s - 1)), as_f32(eT_hi), ALU.subtract
                                            ).then_inc(sem["e_turn_lo"], 1)
                    if s == 1:
                        combined((at, "combine"), 0)
                    if not (last and s == STEPS):
                        used += 2
                        lo_through(min(used + AHEAD, limit))
                        hidden((at, "e_up", s), s)
                    if s == 4 and not last:
                        dve.wait_ge(sem["slots_read"], w.at("slots_read", 2))
                        choose(i + 1, 1)
                    if s == STEPS - 1 and not last:
                        gathered((at, "gather_next"), 2)
                    used += 2
                    lo_through(min(used + AHEAD, limit))
                for c in range(2):
                    dve.wait_ge(sem["os_hi"], w.at("os_hi", c + 1))
                    part = (slice(None), slice(c * BLK, (c + 1) * BLK))
                    nc.vector.scalar_tensor_tensor(os_lo[part], bank((at, "e_down", c)), e_weight, as_f32(os_hi[part]),
                                                   ALU.mult, ALU.subtract).then_inc(sem["os_lo"], 1)
                if last:
                    combined((at, "combine_last"), 4)

            with dve.Fori(0, trip) as i:
                w.item = i
                item("item", i, False)
            w.item = trip
            split[0] = first_loop_unit + AHEAD
            item("last", trip, True)
            mean_square("final", D, NORM_EPS)
            norm(5, "final")

        @block.tensor
        def _(pe):
            w = Count()
            count = [0, 0]

            def ready(key):
                if order.free[key]:
                    reader, n = order.free[key]
                    pe.wait_ge(sem[reader], w.at(reader, n))
                return bank(key)

            def group(mm, *key):
                count[0] += 1
                assert order.done[key] == count[0], key
                mm.then_inc(sem["pe_done"], 1)

            def unit_used(mm, units, *key):
                count[0] += 1
                assert units[count[1]] == count[0] and (not key or order.done[key] == count[0]), key
                count[1] += 1
                mm.then_inc(sem["pe_done"], 1)

            def split_unit(n):
                pe.wait_ge(sem["lo_ready"], w.at("lo_ready", count[1] + 1))
                slot = count[1] % SPLIT_SLOTS
                return (w_hi[:, slot, :].rearrange("p (k n) -> p k n", n=n),
                        w_lo[:, slot, :].rearrange("p (k n) -> p k n", n=n))

            def product(dst, left, k, cols, right, kk, rcols, first, last):
                (l_hi, l_lo), (r_hi, r_lo) = left, right
                nc.tensor.matmul(dst, l_hi[:, k, cols], r_hi[:, kk, rcols], start=first, stop=False)
                nc.tensor.matmul(dst, l_hi[:, k, cols], r_lo[:, kk, rcols], start=False, stop=False)
                return nc.tensor.matmul(dst, l_lo[:, k, cols], r_hi[:, kk, rcols], start=False, stop=last)

            def tokens(t):
                return slice(t * P, (t + 1) * P)

            A = (chunks(actA_hi), chunks(actA_lo))
            B = (chunks(actB_hi), chunks(actB_lo))
            done = order.unit_done

            def project(key, left, n, kc, units, k0=0, u0=0, left0=0):
                per = kc // units
                for u in range(u0, units):
                    right = split_unit(n)
                    for t in range(TILES):
                        if u == 0:
                            ready((*key, t))
                        for kk in range(per):
                            k = u * per + kk
                            mm = product(bank((*key, t))[:, 0:n], left, left0 + k, tokens(t), right, kk, slice(0, n),
                                         k == 0, k == kc - 1)
                        if u == units - 1 and t == 0:
                            group(mm, *key, 0)
                    if u == units - 1:
                        unit_used(mm, done, *key, 1)
                    else:
                        unit_used(mm, done)

            def turn(key, src, n):
                dst = ready(key)
                for m in range(n):
                    mm = nc.tensor.transpose(dst[:, m * P:(m + 1) * P], src[:, m * P:(m + 1) * P], c_("ident"))
                group(mm, *key)

            def turn_norm(n):
                for g in range(4):
                    t, half = divmod(g, 2)
                    pe.wait_ge(sem["hn"], 2 * n + t + 1)
                    turn(("norm_turn", n, g), hn[n][:, t, half * BLK:(half + 1) * BLK], 4)

            def pv(h):
                pe.wait_ge(sem["ret_v"], 2 * h + 2)
                pe.wait_ge(sem["ret_p"], h + 1)
                for t in range(TILES):
                    dst = ready(("ret_pv", h, t))
                    mm = nc.tensor.matmul(dst, r_p[:, h % 2, tokens(t)], r_v[:, h % 2, 0, :], start=True, stop=t == 0)
                    if t:
                        mm = nc.tensor.matmul(dst, r_p[:, h % 2, tokens(2)], r_v[:, h % 2, 1, :], start=False, stop=True)
                    group(mm, "ret_pv", h, t)

            def turn_y(h):
                for t in range(TILES):
                    pe.wait_ge(sem["ret_y"], 2 * h + t + 1)
                    turn(("y_turn", h, t), r_y[:, t, h * RET_DV:(h + 1) * RET_DV], 4)

            pe.wait_ge(sem["const_in"], 16)
            turn_norm(0)
            pe.wait_ge(sem["norm_lo"], 4)
            for j, (kind, n) in enumerate(RET_ORDER):
                pair, stage = divmod(j, 6)
                project(("ret", j), A, BLK, KC, 2)
                if stage == 0 and pair:
                    pv(1)
                if stage in (1, 2):
                    for t in range(TILES):
                        pe.wait_ge(sem["roped"], 2 * (2 * pair + stage - 1) + t + 1)
                        turn(("ret_turn", stage - 1, pair, t), r_rope[stage - 1][:, t, :], 4)
                    if pair:
                        turn_y(stage - 1)
                if stage == 3:
                    pe.wait_ge(sem["ret_turned"], 4 * pair + 4)
                    for h in (2 * pair, 2 * pair + 1):
                        dst, m = ready(("ret_score", h)), 2 * (h % 2)
                        for d in range(2):
                            nc.tensor.matmul(dst[:, 0:SEQ], r_T[1][:, m + d, 0:P], r_T[0][:, m + d, :],
                                             start=d == 0, stop=d == 1)
                        for d in range(2):
                            mm = nc.tensor.matmul(dst[:, SEQ:SEQ + P], r_T[1][:, m + d, P:SEQ], r_T[0][:, m + d, P:SEQ],
                                                  start=d == 0, stop=d == 1)
                        group(mm, "ret_score", h)
                if stage == 5:
                    pv(2 * pair)
            for h in range(RET_H):
                pe.wait_ge(sem["y_lo"], 2 * h + 2)
                for half in range(2):
                    right, last = split_unit(D), h == RET_H - 1 and half == 1
                    for c in range(2):
                        for t in range(TILES):
                            key = ("ret_out", c, t)
                            if h == half == 0:
                                ready(key)
                            for kk in range(2):
                                k = 2 * half + kk
                                mm = product(bank(key), B, 4 * (h % 2) + k, tokens(t), right, kk, slice(c * BLK, (c + 1) * BLK),
                                             h == 0 and k == 0, last and kk == 1)
                            if last and (c, t) != (1, 1):
                                group(mm, *key)
                    unit_used(mm, done, *(("ret_out", 1, 1) if last else ()))
                if h == 0:
                    pv(3)
                    turn_y(2)
                if h == 1:
                    turn_y(3)
            turn_norm(1)
            pe.wait_ge(sem["norm_lo"], 8)
            for s in range(len(blocks) + 1):
                now = s < len(blocks)
                width = blocks[s][1] if now else 0
                n = width * KC // UNIT
                if now and n > 1:
                    right = split_unit(width)
                    for t in range(TILES):
                        ready(("gate", s, t))
                        for k in range(KC // n):
                            mm = product(bank(("gate", s, t))[:, 0:width], A, k, tokens(t), right, k, slice(0, width), k == 0, False)
                    unit_used(mm, done)
                if s:
                    for t in range(TILES):
                        pe.wait_ge(sem["ffn_hid"], 2 * (s - 1) + t + 1)
                        turn(("hid_turn", s - 1, t), f_hid[:, t, :], blocks[s - 1][1] // P)
                if now:
                    project(("gate", s), A, width, KC, n, u0=n - 1)
                for c in range(2):
                    if s:
                        pe.wait_ge(sem["hid_lo"], 2 * s)
                        project(("down", s - 1, c), B, BLK, blocks[s - 1][1] // P, 1)
                    if now and c == 0:
                        project(("up", s), A, width, KC, n)
            turn_norm(2)
            pe.wait_ge(sem["norm_lo"], 12)

            def logits(hp):
                for a in range(2):
                    dst = ready(("logits", hp, 1, a))
                    for part in range(2):
                        mm = nc.tensor.matmul(dst[:, part * SEQ:(part + 1) * SEQ], a_qT[:, part, 2 * hp + a, P:SEQ],
                                              a_kT[:, 2 * hp + a, :], start=True, stop=True)
                    group(mm, "logits", hp, 1, a)
                dst = ready(("logits", hp, 0))
                for m in range(4):
                    mm = nc.tensor.matmul(dst[:, m * P:(m + 1) * P], a_qT[:, m % 2, 2 * hp + m // 2, 0:P],
                                          a_kT[:, 2 * hp + m // 2, 0:P], start=True, stop=True)
                group(mm, "logits", hp, 0)

            for j, (kind, n) in enumerate(KVQ_ORDER):
                if kind == "q" and n == 0:
                    pe.wait_ge(sem["norm_lo"], 16)
                project(("kvq", j), B if kind == "q" else A, BLK, KC, 2)
                if j == 0:
                    turn_norm(3)
                if 1 <= j <= 4:
                    for t in range(TILES):
                        pe.wait_ge(sem["kvq_roped"], 2 * (j - 1) + t + 1)
                        dst = ready(("kvq_turn", j - 1, t))
                        for m in range(4):
                            mm = nc.tensor.transpose(dst[:, m * P:(m + 1) * P], a_rope[:, (j - 1) % 2, t, m * P:(m + 1) * P],
                                                     c_("ident"))
                        group(mm, "kvq_turn", j - 1, t)
                if j == 4:
                    pe.wait_ge(sem["kvq_turned"], 12)
                    logits(0)
            pe.wait_ge(sem["kv_v"], 4)
            for hp in range(PAIRS):
                if hp + 1 < PAIRS:
                    logits(hp + 1)
                for t in (1, 0):
                    pe.wait_ge(sem["attn"], 4 * hp + (2 if t else 4))
                    dst, n = ready(("attn_turn", hp, t)), t + 1
                    for m in range(2 * n):
                        a, keys = divmod(m, n)
                        mm = nc.tensor.transpose(dst[:, m * P:(m + 1) * P], a_a[t][:, a, tokens(keys)], c_("ident"))
                    group(mm, "attn_turn", hp, t)
                    pe.wait_ge(sem["attn_turned"], 2 * hp + 2 - t)
                    key = ("attn_out", hp // 2, t)
                    if hp % 2 == 0:
                        ready(key)
                    for a in range(2):
                        h = 2 * hp + a
                        for keys in range(n):
                            mm = nc.tensor.matmul(bank(key)[:, (h % 4) * P:(h % 4 + 1) * P], a_aT[t][:, a * n + keys, :],
                                                  a_v[:, keys, h * P:(h + 1) * P], start=keys == 0, stop=keys == n - 1)
                    if hp % 2:
                        group(mm, *key)
            for half in range(2):
                for t in range(TILES):
                    pe.wait_ge(sem["attn_o"], 2 * half + t + 1)
                    turn(("o_turn", half, t), a_o[:, t, half * BLK:(half + 1) * BLK], 4)
            pe.wait_ge(sem["o_lo"], 4)
            for c in range(2):
                project(("wo", c), A, BLK, KC, 2)
            turn_norm(4)
            pe.wait_ge(sem["router_x"], 4)
            pe.wait_ge(sem["small_in"], 16 * 6)
            dst = ready(("router",))
            for t in range(TILES):
                for k in range(KC):
                    mm = nc.tensor.matmul(dst[:, t * N_EXPERTS:(t + 1) * N_EXPERTS], e_xT[:, k, tokens(t)], w_router[:, k, :],
                                          start=k == 0, stop=k == KC - 1)
            group(mm, "router")
            pe.wait_ge(sem["chosen"], 1)
            dst = ready(("places",))
            chosen = top[:, 76:92].rearrange("p (t e) -> p t e", t=TILES)
            nc.tensor.matmul(dst[:, 0:8], c_("before"), chosen[:, 0, :], start=True, stop=True)
            nc.tensor.matmul(dst[:, 8:16], c_("ones"), chosen[:, 0, :], start=True, stop=False)
            nc.tensor.matmul(dst[:, 8:16], c_("before"), chosen[:, 1, :], start=False, stop=True)
            nc.tensor.matmul(dst[:, 16:24], c_("ones"), chosen[:, 0, :], start=True, stop=False)
            mm = nc.tensor.matmul(dst[:, 16:24], c_("ones"), chosen[:, 1, :], start=False, stop=True)
            group(mm, "places")

            def gather(key, n):
                pe.wait_ge(sem["choose"], w.at("choose", 2 * n + 2))
                for g in range(2):
                    dst = ready((*key, g))
                    for k in range(4):
                        for t in range(TILES):
                            mm = nc.tensor.matmul(dst[:, k * P:(k + 1) * P], hn[4][:, t, (4 * g + k) * P:(4 * g + k + 1) * P],
                                                  e_choose[:, t, :], start=t == 0, stop=t == TILES - 1)
                    group(mm, *key, g)

            xe = (chunks(xe_hi, P), chunks(xe_lo, P))
            eT = (chunks(eT_hi, P), chunks(eT_lo, P))
            every = slice(0, P)

            def hidden(key, units):
                dst = ready(key)
                for half in range(2):
                    right = split_unit(BLK)
                    for kk in range(4):
                        mm = product(dst, xe, 4 * half + kk, every, right, kk, slice(0, BLK), half == kk == 0, half == 1 and kk == 3)
                    unit_used(mm, units, *(key if half else ()))

            def combine(key, n, f):
                pe.wait_ge(sem["os_lo"], w.at("os_lo", f))
                for q in range(4):
                    t, c = divmod(q, 2)
                    dst = ready((*key, q))
                    nc.tensor.matmul(dst, slots[:, tokens(t)], os_hi[:, c * BLK:(c + 1) * BLK], start=True, stop=False)
                    mm = nc.tensor.matmul(dst, slots[:, tokens(t)], os_lo[:, c * BLK:(c + 1) * BLK], start=False, stop=True)
                    group(mm, *key, q)

            gather(("gather",), 0)
            pe.wait_ge(sem["xe_lo"], w.at("xe_lo", 2))
            hidden(("e_gate", 0), done)
            hidden(("e_up", 0), done)
            pe.wait_ge(sem["routed"], 1)
            trip = pe.value_load(trips[0:1, 0:1], min_val=N_EXPERTS - 1, max_val=2 * N_EXPERTS - 1)
            loop_start = list(count)

            def item(at, last):
                units = done[:first_loop_unit] + (order.last_units if last else order.item_units)
                for s in range(1, STEPS + 1):
                    if not (last and s == STEPS):
                        hidden((at, "e_gate", s), units)
                    pe.wait_ge(sem["e_hid"], w.at("e_hid", s))
                    turn((at, "e_turn", s - 1), e_hid, 4)
                    if s == 1:
                        combine((at, "combine"), 0, 2)
                    if not (last and s == STEPS):
                        hidden((at, "e_up", s), units)
                    if s == 1:
                        dst = ready((at, "slots"))
                        for t in range(TILES):
                            nc.tensor.transpose(dst[:, tokens(t)], e_choose[:, t, :], c_("ident"))
                        for t in range(TILES):
                            mm = nc.tensor.matmul(dst[:, SEQ:SEQ + 1], e_choose[:, t, :], e_cur[:, 2 + t:3 + t],
                                                  start=t == 0, stop=t == TILES - 1)
                        group(mm, at, "slots")
                    if s == STEPS - 1 and not last:
                        gather((at, "gather_next"), 1)
                    pe.wait_ge(sem["e_turn_lo"], w.at("e_turn_lo", s))
                    for half in range(2):
                        right = split_unit(D)
                        end = s == STEPS and half == 1
                        for c in range(2):
                            key = (at, "e_down", c)
                            if s == 1 and half == 0:
                                ready(key)
                            for kk in range(2):
                                mm = product(bank(key), eT, 2 * half + kk, every, right, kk, slice(c * BLK, (c + 1) * BLK),
                                             s == 1 and half == kk == 0, end and kk == 1)
                            if end and c == 0:
                                group(mm, *key)
                        unit_used(mm, units, *(key if end else ()))
                    if s == STEPS - 1 and not last:
                        pe.wait_ge(sem["xe_lo"], w.at("xe_lo", 4))
                if last:
                    combine((at, "combine_last"), 1, 4)

            with pe.Fori(0, trip) as i:
                w.item = i
                item("item", False)
            w.item = trip
            count[:] = loop_start
            item("last", True)


INPUTS = ["x", "attn_norm_g", "ffn_norm_g", "ret_w_in", "ret_w_out", "kv_norm_g", "w_kv", "diff_w_q",
          "diff_lam_q1", "diff_lam_k1", "diff_lam_q2", "diff_lam_k2", "diff_subln_g", "diff_w_o",
          "ffn_w_gate", "ffn_w_up", "ffn_w_down", "moe_w_router", "moe_w_gate", "moe_w_up", "moe_w_down",
          "final_norm_g"]


def kernel(**inputs):
    import concourse.bacc as bacc
    from concourse.bass_utils import run_bass_kernel_spmd

    nc = bacc.Bacc("TRN2", target_bir_lowering=False, num_devices=1)
    arrays, ins = {}, {}
    for name in INPUTS:
        a = np.ascontiguousarray(inputs[name])
        arrays["in_" + name] = a
        ins[name] = nc.dram_tensor("in_" + name, a.shape, mybir.dt.from_np(a.dtype), kind="ExternalInput").ap()
    arrays["constants"] = constant_table()
    table = nc.dram_tensor("constants", arrays["constants"].shape, F32, kind="ExternalInput").ap()
    out = nc.dram_tensor("out", (1, SEQ, D), F32, kind="ExternalOutput").ap()
    stream(nc, ins, out, table)
    r = run_bass_kernel_spmd(nc, [arrays], core_ids=[0])
    return r.results[0]["out"]
```
